# Optimizing a Trainium2 kernel written in Bass

```python
import jax
import jax.numpy as jnp
from jax import lax
import numpy as np

D_MODEL = 1024
BATCH = 1
SEQ = 256
DEPTH = 1

EPS = 1e-6
ROPE_THETA = 10000.0
Q_BLOCK = 128

A_HEADS = 8
A_HEAD_DIM = 64
A_WIDTH = A_HEADS * A_HEAD_DIM
MOBA_BLOCK = 256
MOBA_TOPK = 3

B_HEADS = 8
B_NOPE = 64
B_ROPE = 32
B_QK = B_NOPE + B_ROPE
B_V = 64
B_Q_RANK = 384
B_KV_RANK = 256
B_WIDTH = B_HEADS * B_V

D_FF = 4 * D_MODEL

IN_SPLITS = (A_WIDTH, A_WIDTH, A_WIDTH, B_Q_RANK, B_KV_RANK, B_ROPE, D_MODEL, D_MODEL)
IN_WIDTH = sum(IN_SPLITS)

kernel_name = "hybrid_gated_moba_mla_block"

def rmsnorm(x, g):
    xf = x.astype(jnp.float32)
    y = xf * lax.rsqrt(jnp.mean(xf * xf, axis=-1, keepdims=True) + EPS)
    return (y * g.astype(jnp.float32)).astype(x.dtype)

def rope(x, pos):
    half = x.shape[-1] // 2
    inv_freq = jnp.power(ROPE_THETA, -jnp.arange(half, dtype=jnp.float32) / half)
    ang = pos.astype(jnp.float32)[:, None] * inv_freq[None, :]
    cos = jnp.cos(ang)[None, :, None, :]
    sin = jnp.sin(ang)[None, :, None, :]
    xf = x.astype(jnp.float32)
    x1, x2 = xf[..., :half], xf[..., half:]
    return jnp.concatenate([x1 * cos - x2 * sin, x2 * cos + x1 * sin], axis=-1).astype(x.dtype)

def moba_attention(q, k, v):
    b, h, s, dh = q.shape
    nb = -(-s // MOBA_BLOCK)
    pad = nb * MOBA_BLOCK - s
    padw = ((0, 0), (0, 0), (0, pad), (0, 0))
    kb = jnp.pad(k, padw).reshape(b, h, nb, MOBA_BLOCK, dh)
    vb = jnp.pad(v, padw).reshape(b, h, nb, MOBA_BLOCK, dh)
    k_mean = jnp.mean(kb.astype(jnp.float32), axis=3)
    topk = min(MOBA_TOPK, nb)
    scale = dh ** -0.5
    bi = jnp.arange(b)[:, None, None, None]
    hi = jnp.arange(h)[None, :, None, None]
    blk_ids = jnp.arange(nb)
    in_blk = jnp.arange(MOBA_BLOCK)

    def one_chunk(c):
        start = c * Q_BLOCK
        qc = lax.dynamic_slice_in_dim(q, start, Q_BLOCK, axis=2)
        qpos = start + jnp.arange(Q_BLOCK)
        qblk = start // MOBA_BLOCK
        gate = jnp.einsum('bhtd,bhnd->bhtn', qc.astype(jnp.float32), k_mean)
        gate = jnp.where(blk_ids < qblk, gate, -jnp.inf)
        _, sel = lax.top_k(gate, topk)
        valid = sel < qblk
        k_sel = kb[bi, hi, sel]
        v_sel = vb[bi, hi, sel]
        k_own = lax.dynamic_index_in_dim(kb, qblk, axis=2, keepdims=False)
        v_own = lax.dynamic_index_in_dim(vb, qblk, axis=2, keepdims=False)
        own_mask = (qblk * MOBA_BLOCK + in_blk)[None, :] <= qpos[:, None]
        s_sel = jnp.einsum('bhtd,bhtkld->bhtkl', qc, k_sel,
                           preferred_element_type=jnp.float32) * scale
        s_sel = jnp.where(valid[..., None], s_sel, -jnp.inf)
        s_own = jnp.einsum('bhtd,bhld->bhtl', qc, k_own,
                           preferred_element_type=jnp.float32) * scale
        s_own = jnp.where(own_mask, s_own, -jnp.inf)
        scores = jnp.concatenate(
            [s_sel.reshape(b, h, Q_BLOCK, topk * MOBA_BLOCK), s_own], axis=-1)
        p = jax.nn.softmax(scores, axis=-1).astype(v.dtype)
        p_sel = p[..., :topk * MOBA_BLOCK].reshape(b, h, Q_BLOCK, topk, MOBA_BLOCK)
        p_own = p[..., topk * MOBA_BLOCK:]
        return (jnp.einsum('bhtkl,bhtkld->bhtd', p_sel, v_sel)
                + jnp.einsum('bhtl,bhld->bhtd', p_own, v_own))

    out = lax.map(one_chunk, jnp.arange(s // Q_BLOCK))
    return jnp.moveaxis(out, 0, 2).reshape(b, h, s, dh)

def mla_attention(q_nope, q_rope, k_nope, k_rope, v):
    b, h, s, _ = q_nope.shape
    scale = B_QK ** -0.5
    kpos = jnp.arange(s)

    def one_chunk(c):
        start = c * Q_BLOCK
        qn = lax.dynamic_slice_in_dim(q_nope, start, Q_BLOCK, axis=2)
        qr = lax.dynamic_slice_in_dim(q_rope, start, Q_BLOCK, axis=2)
        qpos = start + jnp.arange(Q_BLOCK)
        sc = (jnp.einsum('bhtd,bhsd->bhts', qn, k_nope, preferred_element_type=jnp.float32)
              + jnp.einsum('bhtd,bsd->bhts', qr, k_rope, preferred_element_type=jnp.float32)) * scale
        sc = jnp.where(kpos[None, :] <= qpos[:, None], sc, -jnp.inf)
        p = jax.nn.softmax(sc, axis=-1).astype(v.dtype)
        return jnp.einsum('bhts,bhsd->bhtd', p, v)

    out = lax.map(one_chunk, jnp.arange(s // Q_BLOCK))
    return jnp.moveaxis(out, 0, 2).reshape(b, h, s, v.shape[-1])

def setup_inputs(seed: int = 0) -> dict:
    key = jax.random.key(seed)
    ks = jax.random.split(key, 15)

    def dense(k, fan_in, shape):
        return jax.random.normal(k, shape, jnp.float32) * fan_in ** -0.5

    def gain(k, shape):
        return 1.0 + 0.02 * jax.random.normal(k, shape, jnp.float32)

    return {
        "x": jax.random.normal(ks[0], (BATCH, SEQ, D_MODEL), jnp.float32),
        "g_mix": gain(ks[1], (DEPTH, D_MODEL)),
        "w_in": dense(ks[2], D_MODEL, (DEPTH, D_MODEL, IN_WIDTH)),
        "b_gate": 0.02 * jax.random.normal(ks[3], (DEPTH, 2, D_MODEL), jnp.float32),
        "g_cq": gain(ks[4], (DEPTH, B_Q_RANK)),
        "w_q_up": dense(ks[5], B_Q_RANK, (DEPTH, B_Q_RANK, B_HEADS * B_QK)),
        "g_ckv": gain(ks[6], (DEPTH, B_KV_RANK)),
        "w_kv_up": dense(ks[7], B_KV_RANK, (DEPTH, B_KV_RANK, B_HEADS * (B_NOPE + B_V))),
        "w_o_a": dense(ks[8], A_WIDTH, (DEPTH, A_WIDTH, D_MODEL)),
        "w_o_b": dense(ks[9], B_WIDTH, (DEPTH, B_WIDTH, D_MODEL)),
        "w_out": dense(ks[10], D_MODEL, (DEPTH, D_MODEL, D_MODEL)),
        "g_mlp": gain(ks[11], (DEPTH, D_MODEL)),
        "w_ff1": dense(ks[12], D_MODEL, (DEPTH, D_MODEL, D_FF)),
        "w_ff2": dense(ks[13], D_FF, (DEPTH, D_FF, D_MODEL)),
        "g_final": gain(ks[14], (D_MODEL,)),
    }

def reference(x, g_mix, w_in, b_gate, g_cq, w_q_up, g_ckv, w_kv_up, w_o_a, w_o_b,
              w_out, g_mlp, w_ff1, w_ff2, g_final):
    b, s, _ = x.shape
    pos = jnp.arange(s)
    offsets = [int(o) for o in np.cumsum(IN_SPLITS)[:-1]]
    for l in range(DEPTH):
        h = rmsnorm(x, g_mix[l])
        proj = jnp.einsum('bsd,de->bse', h, w_in[l])
        qa, ka, va, cq, ckv, kr, gate_a, gate_b = jnp.split(proj, offsets, axis=-1)

        qa = rope(qa.reshape(b, s, A_HEADS, A_HEAD_DIM), pos).transpose(0, 2, 1, 3)
        ka = rope(ka.reshape(b, s, A_HEADS, A_HEAD_DIM), pos).transpose(0, 2, 1, 3)
        va = va.reshape(b, s, A_HEADS, A_HEAD_DIM).transpose(0, 2, 1, 3)
        o_a = moba_attention(qa, ka, va).transpose(0, 2, 1, 3).reshape(b, s, A_WIDTH)

        qb = jnp.einsum('bsr,re->bse', rmsnorm(cq, g_cq[l]), w_q_up[l]).reshape(b, s, B_HEADS, B_QK)
        q_nope = qb[..., :B_NOPE].transpose(0, 2, 1, 3)
        q_rope = rope(qb[..., B_NOPE:], pos).transpose(0, 2, 1, 3)
        kv = jnp.einsum('bsr,re->bse', rmsnorm(ckv, g_ckv[l]), w_kv_up[l]).reshape(
            b, s, B_HEADS, B_NOPE + B_V)
        k_nope = kv[..., :B_NOPE].transpose(0, 2, 1, 3)
        v_b = kv[..., B_NOPE:].transpose(0, 2, 1, 3)
        k_rope = rope(kr[:, :, None, :], pos)[:, :, 0, :]
        o_b = mla_attention(q_nope, q_rope, k_nope, k_rope, v_b).transpose(0, 2, 1, 3).reshape(
            b, s, B_WIDTH)

        y_a = jnp.einsum('bse,ed->bsd', o_a, w_o_a[l])
        y_b = jnp.einsum('bse,ed->bsd', o_b, w_o_b[l])
        g_a = jax.nn.sigmoid(gate_a + b_gate[l, 0])
        g_b = jax.nn.sigmoid(gate_b + b_gate[l, 1])
        x = x + jnp.einsum('bsd,de->bse', g_a * y_a + g_b * y_b, w_out[l])

        h2 = rmsnorm(x, g_mlp[l])
        u = jax.nn.relu(jnp.einsum('bsd,df->bsf', h2, w_ff1[l]))
        x = x + jnp.einsum('bsf,fd->bsd', u * u, w_ff2[l])
    return rmsnorm(x, g_final)


_drawn_inputs = setup_inputs


def setup_inputs(seed=0):
    import zlib

    import numpy as np

    out = dict(_drawn_inputs(seed))
    spreads = {}
    factors = {'g_mix': 8.0, 'b_gate': 8.0, 'g_cq': 8.0, 'g_ckv': 8.0, 'g_mlp': 9.054, 'g_final': 8.278}
    for name, (base, spread) in spreads.items():
        noise = np.random.default_rng([zlib.crc32(name.encode()), seed]).standard_normal(out[name].shape)
        drawn = base * np.exp(spread * noise) if base else spread * noise
        out[name] = jnp.asarray(drawn.astype(out[name].dtype))
    for name, factor in factors.items():
        out[name] = (out[name] * factor).astype(out[name].dtype)
    return out
```

```python
from contextlib import ExitStack

import numpy as np
import concourse.bass as bass
from concourse import mybir

F32 = mybir.dt.float32
F32R = mybir.dt.float32r
BF16 = mybir.dt.bfloat16
ALU = mybir.AluOpType
ACT = mybir.ActivationFunctionType
AX_X = mybir.AxisListType.X

P = 128
SEQ, D = 256, 1024
TT = SEQ // P
KT = D // P
A_HEADS, A_DIM = 8, 64
A_WIDTH = A_HEADS * A_DIM
B_HEADS, B_NOPE, B_ROPE, B_V = 8, 64, 32, 64
B_QK = B_NOPE + B_ROPE
Q_RANK, KV_RANK = 384, 256
D_FF = 4 * D
EPS = 1e-6
ROPE_THETA = 10000.0
SCALE_A = float(A_DIM) ** -0.5
SCALE_B = float(B_QK) ** -0.5
MASKED = -3.0e38
HALF = 512

COL_QA, COL_KA, COL_VA = 0, A_WIDTH, 2 * A_WIDTH
COL_CQ = 3 * A_WIDTH
COL_CKV = COL_CQ + Q_RANK
CKV_W = KV_RANK + B_ROPE
COL_GATE = COL_CKV + CKV_W

CQ, CKV, KA, QA, VA, QB0, QB1, KVB0, KVB1, GATE0 = range(10)
NGATE = 2 * D // HALF
CHUNKS = GATE0 + NGATE
SHAPE = {CQ: (Q_RANK, KT), CKV: (CKV_W, KT), KA: (HALF, KT), QA: (HALF, KT), VA: (HALF, KT),
         QB0: (4 * B_QK, 3), QB1: (4 * B_QK, 3), KVB0: (HALF, 2), KVB1: (HALF, 2)}
SHAPE.update({GATE0 + n: (HALF, KT) for n in range(NGATE)})

SLOTS = 4
SLOT_W = 2048
UNITS_OF = {}
_u = 0
for _c in range(CHUNKS):
    _n = 2 if SHAPE[_c][1] == KT else 1
    UNITS_OF[_c] = (_u, _n, SHAPE[_c][1] // _n)
    _u += _n
U_GATE = UNITS_OF[GATE0][0]
U_WO = _u
U_OUT = U_WO + 4
U_FF = U_OUT + 4
FF_CHUNKS = D_FF // HALF
UNITS = U_FF + 4 * FF_CHUNKS
AHEAD = SLOTS - 1

HEAD_ORDER = (0, 2, 4, 6, 1, 3, 5, 7)
GROUPS = [(path, t, HEAD_ORDER[h:h + (4 >> t)]) for path in range(2) for t in range(TT)
          for h in range(0, 8, 4 >> t)]
NG = len(GROUPS)
G_SLOT = 1
STEPS = 4 * NGATE
O_GROUP = [max(g for g in range(NG) if GROUPS[g][:2] == (path, t)) for path in range(2) for t in range(TT)]
O_STEP = [g + G_SLOT + 3 for g in O_GROUP]
QK_BANK = (7, 4, 5, 6)
Y_BANK = (2, 0, 2, 0)
WARM_UP = 36
ROW_BANK = (2, 3, 0, 1)


def rope_tables(dim):
    half = dim // 2
    inv = np.power(np.float32(ROPE_THETA), -np.arange(half, dtype=np.float32) / np.float32(half))
    ang = np.arange(SEQ, dtype=np.float32)[:, None] * inv.astype(np.float32)[None, :]
    cos, sin = np.cos(ang).astype(np.float32), np.sin(ang).astype(np.float32)
    c = np.concatenate([cos, cos], axis=1).reshape(TT, P, dim).transpose(1, 0, 2)
    s = np.concatenate([-sin, sin], axis=1).reshape(TT, P, dim).transpose(1, 0, 2)
    return np.ascontiguousarray(np.stack([c, s], axis=1))


def hybrid_block(nc, x, g_mix, w_in, b_gate, g_cq, w_q_up, g_ckv, w_kv_up, w_o_a, w_o_b, w_out,
                 g_mlp, w_ff1, w_ff2, g_final, rope_a, rope_b, out):
    x_v = x[0].rearrange("(t p) d -> p t d", p=P)
    out_v = out[0].rearrange("(t p) d -> p t d", p=P)
    w_in_v = w_in[0].rearrange("(k p) n -> p k n", p=P)
    w_q_v = w_q_up[0].rearrange("(k p) n -> p k n", p=P)
    w_kv_v = w_kv_up[0].rearrange("(k p) n -> p k n", p=P)
    w_o_v = [w_o_a[0].rearrange("(k p) n -> p k n", p=P), w_o_b[0].rearrange("(k p) n -> p k n", p=P)]
    w_out_v = w_out[0].rearrange("(k p) n -> p k n", p=P)
    w1_v = w_ff1[0].rearrange("(k p) n -> p k n", p=P)

    with ExitStack() as ctx:
        def sb(name, shape, dt):
            return ctx.enter_context(nc.sbuf_tensor(name, shape, dt))

        def sem(name):
            return ctx.enter_context(nc.semaphore(name))

        raw = sb("raw", [P, SLOTS, SLOT_W], F32)
        whi = sb("whi", [P, SLOTS, SLOT_W], F32R)
        wlo = sb("wlo", [P, SLOTS, SLOT_W], F32R)
        xs = sb("xs", [P, TT, D], F32)
        xT_hi = sb("xT_hi", [P, KT, SEQ], F32R)
        xT_lo = sb("xT_lo", [P, KT, SEQ], F32R)
        lat_hi = sb("lat_hi", [P, 8, SEQ], F32R)
        lat_lo = sb("lat_lo", [P, 8, SEQ], F32R)
        gates = sb("gates", [P, TT, 2 * D], F32)
        v_a = sb("v_a", [P, TT, A_WIDTH], F32)
        v_b = sb("v_b", [P, TT, B_HEADS * B_V], F32)
        qkT_a = sb("qkT_a", [P, 2, 4, SEQ], F32)
        qkT_b = sb("qkT_b", [P, 2, 8, SEQ], F32)
        rows = sb("rows", [P, 4, HALF], F32)
        prob = sb("prob", [P, 4, HALF], F32)
        k_rope = sb("k_rope", [P, TT, B_ROPE], F32)
        k_tmp = sb("k_tmp", [P, 2, B_ROPE], F32)
        tab_a = sb("tab_a", [P, 2, TT, A_DIM], F32)
        tab_b = sb("tab_b", [P, 2, TT, B_ROPE], F32)
        ident = sb("ident", [P, P], F32)
        ident_h = sb("ident_h", [P, P], BF16)
        causal = sb("causal", [P, P], BF16)
        gcol = sb("gcol", [P, KT + 3 + 2], F32)
        neg_half = sb("neg_half", [P, TT], F32)
        ssq = sb("ssq", [P, 14], F32)
        var = sb("var", [P, 12], F32)
        rstd = sb("rstd", [P, 16], F32)
        negmax = sb("negmax", [P, NG, 4], F32)
        rowsum = sb("rowsum", [P, 4, 8], F32)
        rrow = sb("rrow", [P, 4, 8], F32)
        ps = ctx.enter_context(nc.psum_tensor("ps", [P, 8, HALF], F32))

        N_MIX, N_CQ, N_CKV, N_MLP, N_FIN = 0, 2, 4, 6, 8
        R_QA, R_QB = 10, 12
        SSQ_MLP, SSQ_FIN = 6, 10
        cq_rows = gates[:, 1, 0:TT * Q_RANK].rearrange("p (t n) -> p t n", t=TT)
        ckv_rows = gates[:, 1, TT * Q_RANK:TT * (Q_RANK + KV_RANK)].rearrange("p (t n) -> p t n", t=TT)
        g_mlp_row = qkT_b[:, 1, 0:4, :].rearrange("p a b -> p (a b)")
        g_fin_row = qkT_b[:, 1, 4:8, :].rearrange("p a b -> p (a b)")
        oT_hi = lat_hi[:, :, :].rearrange("p (path k) s -> p path k s", path=2)
        oT_lo = lat_lo[:, :, :].rearrange("p (path k) s -> p path k s", path=2)
        final_rows = qkT_b[:, 0, :, :].rearrange("p (t a) b -> p t (a b)", t=TT)

        x_landed = [sem(f"x_landed{t}") for t in range(TT)]
        gmix_landed = sem("gmix_landed")
        gcol_landed = sem("gcol_landed")
        tab_landed = sem("tab_landed")
        bias_landed = sem("bias_landed")
        grow_landed = sem("grow_landed")
        first_landed = sem("first_landed")
        raw_landed = [sem(f"raw_landed{s}") for s in range(SLOTS)]
        out_stored = sem("out_stored")
        zeroed = sem("zeroed")
        const_ready = sem("const_ready")
        whi_ready = sem("whi_ready")
        wlo_ready = sem("wlo_ready")
        chunk_half = sem("chunk_half")
        w2_used = sem("w2_used")
        x_turned = sem("x_turned")
        xT_hi_done = sem("xT_hi_done")
        xT_lo_done = sem("xT_lo_done")
        chunk_done = sem("chunk_done")
        act_read = sem("act_read")
        ssq_done = sem("ssq_done")
        var_done = sem("var_done")
        rstd_done = sem("rstd_done")
        lat_rows = sem("lat_rows")
        latT = sem("latT")
        latT_hi = sem("latT_hi")
        latT_lo = sem("latT_lo")
        rope_part = sem("rope_part")
        rows_dve = sem("rows_dve")
        rows_act = sem("rows_act")
        krope_done = sem("krope_done")
        qk_turned = sem("qk_turned")
        qkT_ready = sem("qkT_ready")
        scored = sem("scored")
        max_ready = sem("max_ready")
        p_ready = sem("p_ready")
        p_turned = sem("p_turned")
        pT_ready = sem("pT_ready")
        pv_done = sem("pv_done")
        rrow_ready = sem("rrow_ready")
        o_rows = sem("o_rows")
        o_turned = sem("o_turned")
        oT_hi_done = sem("oT_hi_done")
        oT_lo_done = sem("oT_lo_done")
        gate_lin = sem("gate_lin")
        gate_done = sem("gate_done")
        y_done = sem("y_done")
        m_part = sem("m_part")
        m_rows = sem("m_rows")
        m_turned = sem("m_turned")
        mT_hi = sem("mT_hi")
        mT_lo = sem("mT_lo")
        mix_done = sem("mix_done")
        res_done = sem("res_done")
        h_rows = sem("h_rows")
        h_turned = sem("h_turned")
        hT_hi = sem("hT_hi")
        hT_lo = sem("hT_lo")
        u_done = sem("u_done")
        u_relu = sem("u_relu")
        u_sq = sem("u_sq")
        u_turned = sem("u_turned")
        uT_hi_done = sem("uT_hi_done")
        uT_lo_done = sem("uT_lo_done")
        ff_done = sem("ff_done")
        fin_res = sem("fin_res")
        fin_scaled = sem("fin_scaled")
        fin_rows = sem("fin_rows")
        fin_rows_act = sem("fin_rows_act")
        out_stored_act = sem("out_stored_act")

        ACT_READ = {CQ: (lat_rows, 2), CKV: (lat_rows, 4), VA: (act_read, 2), QB0: (rows_act, 2),
                    QB1: (rows_act, 4), KVB0: (rows_act, 6), KVB1: (rows_act, 8)}
        DVE_READ = {CKV: (krope_done, 2), KA: (rows_dve, 2), QA: (rows_dve, 4), QB0: (rows_dve, 6),
                    QB1: (rows_dve, 8)}
        DVE_READ.update({GATE0 + q: (gate_lin, TT * (q + 1)) for q in range(NGATE)})

        def used(u):
            for c in range(CHUNKS):
                first, n, _ = UNITS_OF[c]
                if first <= u < first + n:
                    if u < first + n - 1:
                        return chunk_half, 1 + sum(UNITS_OF[b][1] == 2 for b in range(c))
                    return chunk_done, TT * (c + 1)
            if u < U_OUT:
                return y_done, 4 + u - U_WO + 1
            if u < U_FF:
                return mix_done, 3 + (u - U_OUT) // 2
            return (u_done, 2) if u < U_FF + 2 else (w2_used, u - U_FF - 1)

        def bcast(ap, n):
            return ap.unsqueeze(1).broadcast_to([P, n, ap.shape[-1]])

        def unit_source(u):
            for c in range(CHUNKS):
                first, n, kts = UNITS_OF[c]
                if first <= u < first + n:
                    k0, w = (u - first) * kts, SHAPE[c][0]
                    if c in (QB0, QB1):
                        return w_q_v[:, :, (c - QB0) * w:(c - QB0 + 1) * w]
                    if c in (KVB0, KVB1):
                        return w_kv_v[:, :, (c - KVB0) * w:(c - KVB0 + 1) * w]
                    col = {CQ: COL_CQ, CKV: COL_CKV, KA: COL_KA, QA: COL_QA, VA: COL_VA}.get(
                        c, COL_GATE + (c - GATE0) * HALF)
                    return w_in_v[:, k0:k0 + kts, col:col + w]
            if u < U_OUT:
                n, path = divmod(u - U_WO, 2)
                return w_o_v[path][:, :, n * HALF:(n + 1) * HALF]
            n, k = divmod(u - U_OUT, 2)
            return w_out_v[:, 4 * k:4 * k + 4, n * HALF:(n + 1) * HALF]

        def unit_width(u):
            if u >= U_FF:
                return SLOT_W
            s = unit_source(u).shape
            return s[1] * s[2]

        block = ctx.enter_context(nc.Block())

        @block.sync
        def _(sp):
            def load_unit(u):
                s, src = u % SLOTS, unit_source(u)
                dst = raw[:, s, 0:unit_width(u)].rearrange("p (k n) -> p k n", k=src.shape[1])
                if u >= SLOTS:
                    sp.wait_ge(wlo_ready, 2 * (u - SLOTS) + 2)
                if u == 0:
                    half = src.shape[1] // 2
                    sp.dma_start(dst[:, 0:half, :], src[:, 0:half, :]).then_inc(first_landed, 16)
                    dst, src = dst[:, half:, :], src[:, half:, :]
                sp.dma_start(dst, src).then_inc(raw_landed[s], 16)

            def load_ff(c, j):
                s = (U_FF + j) % SLOTS
                sp.wait_ge(wlo_ready, (c * 8) + 2 * (U_FF + j - SLOTS) + 2)
                if j < 2:
                    src = w1_v[:, :, bass.ds(c * HALF + j * 256, 256)]
                    dst = raw[:, s, :].rearrange("p (k n) -> p k n", k=KT)
                else:
                    src = w_ff2[0, bass.ds(c * HALF + (j - 2) * 256, 256), :].rearrange(
                        "(f p) n -> p f n", p=P)
                    dst = raw[:, s, :].rearrange("p (k n) -> p k n", k=2)
                sp.dma_start(dst, src).then_inc(raw_landed[s], 16)

            for t in range(TT):
                sp.dma_start(xs[:, t, :], x_v[:, t, :]).then_inc(x_landed[t], 16)
            for u in range(U_FF):
                load_unit(u)
            with sp.Fori(0, FF_CHUNKS) as c:
                for j in range(4):
                    load_ff(c, j)
            sp.wait_ge(fin_rows_act, 1)
            sp.dma_start(out_v[:, 0, HALF:D], final_rows[:, 0, HALF:D]).then_inc(out_stored, 16)
            for t in range(TT):
                sp.wait_ge(fin_rows, t + 1)
                sp.dma_start(out_v[:, t, 0:HALF], final_rows[:, t, 0:HALF]).then_inc(out_stored, 16)
            sp.wait_ge(out_stored, 16 * (TT + 1))
            sp.wait_ge(out_stored_act, 16)

        @block.gpsimd
        def _(pool):
            pool.memset(ident[:, :], 0.0).then_inc(zeroed, 1)
            pool.memset(ident_h[:, :], 0.0).then_inc(zeroed, 1)
            pool.memset(causal[:, :], 0.0).then_inc(zeroed, 1)
            pool.memset(neg_half[:, :], -0.5).then_inc(zeroed, 1)
            pool.wait_ge(zeroed, 4)
            for m in (ident, ident_h):
                pool.affine_select(out=m[:, :], in_=m[:, :], compare_op=ALU.not_equal, fill=1.0, base=0,
                                   pattern=[[-1, P]], channel_multiplier=1).then_inc(const_ready, 1)
            pool.affine_select(out=causal[:, :], in_=causal[:, :], compare_op=ALU.is_ge, fill=MASKED, base=0,
                               pattern=[[-1, P]], channel_multiplier=1).then_inc(const_ready, 1)
            with nc.allow_non_contiguous_dma(reason="columns of gains, a few KB"):
                pool.dma_start(gcol[:, KT:KT + 3], g_cq[0].rearrange("(k p) -> p k", p=P)).then_inc(gcol_landed, 16)
                pool.dma_start(gcol[:, KT + 3:KT + 5], g_ckv[0].rearrange("(k p) -> p k", p=P)).then_inc(gcol_landed, 16)
            pool.dma_start(tab_a[:, :, :, :], rope_a).then_inc(tab_landed, 16)
            pool.dma_start(tab_b[:, :, :, :], rope_b).then_inc(tab_landed, 16)

            n_var = [0]
            n_rstd = [0]

            def inverse_root(src, dst, w, width, rest=EPS):
                pool.tensor_scalar(var[:, dst:dst + w], src, 1.0 / width, rest, ALU.mult,
                                   ALU.add).then_inc(var_done, 1)
                n_var[0] += 1
                pool.wait_ge(var_done, n_var[0])
                pool.tensor_tensor(rstd[:, dst:dst + w], var[:, dst:dst + w], neg_half[:, 0:w],
                                   ALU.pow).then_inc(rstd_done, 1)
                n_rstd[0] += 1
                pool.wait_ge(rstd_done, n_rstd[0])

            def scaled(src, dst, factor):
                pool.tensor_scalar(rstd[:, dst:dst + TT], rstd[:, src:src + TT], factor, None,
                                   ALU.mult).then_inc(rstd_done, 1)
                n_rstd[0] += 1

            pool.wait_ge(ssq_done, 2)
            inverse_root(ssq[:, N_MIX:N_MIX + TT], N_MIX, TT, D)
            scaled(N_MIX, R_QA, SCALE_A)
            pool.wait_ge(ssq_done, 4)
            inverse_root(ssq[:, N_CQ:N_CQ + TT], N_CQ, TT, Q_RANK)
            scaled(N_CQ, R_QB, SCALE_B)
            pool.wait_ge(ssq_done, 6)
            inverse_root(ssq[:, N_CKV:N_CKV + TT], N_CKV, TT, KV_RANK)
            pool.wait_ge(latT, 3)
            b_row = b_gate[0].rearrange("a d -> (a d)")
            for t in range(TT):
                pool.dma_start(gates[:, t, :], b_row.partition_broadcast(P)).then_inc(bias_landed, 16)
            pool.wait_ge(scored, NG)
            pool.dma_start(g_mlp_row, g_mlp[0].partition_broadcast(P)).then_inc(grow_landed, 16)
            pool.dma_start(g_fin_row, g_final.partition_broadcast(P)).then_inc(grow_landed, 16)
            for base, src, dst in ((6, SSQ_MLP, N_MLP), (10, SSQ_FIN, N_FIN)):
                for t in range(TT):
                    first = ssq[:, src + 2 * t:src + 2 * t + 1]
                    pool.wait_ge(ssq_done, base + 2 * t + 1)
                    pool.tensor_scalar(var[:, 10:11], first, 1.0 / D, EPS, ALU.mult, ALU.add).then_inc(var_done, 1)
                    n_var[0] += 1
                    pool.wait_ge(var_done, n_var[0])
                    pool.wait_ge(ssq_done, base + 2 * t + 2)
                    inverse_root(ssq[:, src + 2 * t + 1:src + 2 * t + 2], dst + t, 1, D, var[:, 10:11])

        RSTD_MIX, RSTD_QA, RSTD_CQ, RSTD_QB, RSTD_CKV, RSTD_MLP, RSTD_FIN = 1, 2, 3, 4, 5, 6, 8

        @block.scalar
        def _(act):
            def copy(dst, src, scale=1.0):
                return nc.scalar.activation(dst, src, ACT.Copy, scale=scale)

            def high(u, h):
                s, w = u % SLOTS, unit_width(u) // 2
                if u == 0:
                    act.wait_ge((first_landed, raw_landed[0])[h], 16)
                elif h == 0:
                    act.wait_ge(raw_landed[s], 16 * (u // SLOTS + 1))
                    if u >= SLOTS:
                        act.wait_ge(*used(u - SLOTS))
                copy(whi[:, s, h * w:(h + 1) * w], raw[:, s, h * w:(h + 1) * w]).then_inc(whi_ready, 1)

            def high_unit(u):
                high(u, 0)
                high(u, 1)

            def squares(src, n, col, junk):
                nc.scalar.activation(junk, src, ACT.Square, accum_out=ssq[:, col:col + 1]).then_inc(ssq_done, 1)

            def chunk(c, t):
                act.wait_ge(chunk_done, TT * c + t + 1)
                return ps[:, 2 * (c % 2) + t, 0:SHAPE[c][0]]

            def qkT_copy(e):
                act.wait_ge(qk_turned, e + 1)
                bank = QK_BANK[e % 4]
                src = ps[:, bank, :].rearrange("p (b s) -> p b s", b=4)
                if e < 4:
                    which, t = 1 - e // 2, e % 2
                    copy(qkT_a[:, which, :, t * P:(t + 1) * P], src).then_inc(qkT_ready, 1)
                else:
                    which, c, t = (e - 4) // 4, (e - 4) % 4 // 2, e % 2
                    copy(qkT_b[0:B_QK, which, 4 * c:4 * c + 4, t * P:(t + 1) * P],
                         src[0:B_QK, :, :]).then_inc(qkT_ready, 1)

            def up_rows(c, t):
                src = chunk(c, t).rearrange("p (h n) -> p h n", h=4)
                slot = 2 * ((c - QB0) % 2) + t
                dst = rows[:, slot, 0:4 * B_QK].rearrange("p (h n) -> p h n", h=4)
                if c >= KVB0:
                    act.wait_ge(qk_turned, 4 + 2 * (c - KVB0) + t + 1)
                    act.wait_ge(rstd_done, RSTD_CKV)
                    r = rstd[:, N_CKV + t:N_CKV + t + 1]
                    h = 4 * (c - KVB0)
                    copy(v_b[:, t, h * B_V:(h + 4) * B_V].rearrange("p (h n) -> p h n", h=4),
                         src[:, :, B_NOPE:B_NOPE + B_V], r)
                else:
                    act.wait_ge(qk_turned, 2 * (c - QB0) + t + 1)
                    act.wait_ge(rstd_done, RSTD_QB)
                    r = rstd[:, R_QB + t:R_QB + t + 1]
                copy(dst[:, :, 0:B_NOPE], src[:, :, 0:B_NOPE], r).then_inc(rows_act, 1)

            def up_both(c):
                up_rows(c, 0)
                up_rows(c, 1)

            with nc.allow_non_contiguous_dma(reason="a column of gains, 4 KB"):
                act.dma_start(gcol[:, 0:KT], g_mix[0].rearrange("(k p) -> p k", p=P)).then_inc(gmix_landed, 16)
            act.wait_ge(zeroed, 4)
            nc.scalar.activation(rrow[:, 0, 0:TT], neg_half[:, :], ACT.Exp)
            act.wait_ge(x_landed[0], 16)
            squares(xs[:, 0, :], D, N_MIX, rows[:, 0:2, :].rearrange("p a b -> p (a b)"))
            act.wait_ge(gmix_landed, 16)
            for k in range(KT):
                if k % 2 == 0:
                    act.wait_ge(x_turned, k // 2 + 1)
                copy(xT_hi[:, k, :], ps[:, 4 + k // 2, (k % 2) * SEQ:(k % 2 + 1) * SEQ],
                     gcol[:, k:k + 1]).then_inc(xT_hi_done, 1)
                if k in (1, 3):
                    high(0, k // 2)
            high_unit(1)
            act.wait_ge(x_landed[1], 16)
            squares(xs[:, 1, :], D, N_MIX + 1, rows[:, 2:4, :].rearrange("p a b -> p (a b)"))
            high_unit(2)
            high_unit(3)
            high_unit(4)
            act.wait_ge(rstd_done, RSTD_MIX)
            for t in range(TT):
                copy(cq_rows[:, t, :], chunk(CQ, t), rstd[:, N_MIX + t:N_MIX + t + 1]).then_inc(lat_rows, 1)
            act.wait_ge(lat_rows, 2)
            for t in range(TT):
                squares(cq_rows[:, t, :], Q_RANK, N_CQ + t, prob[:, 2 + t, 0:Q_RANK])
            high_unit(5)
            high_unit(6)
            for t in range(TT):
                copy(ckv_rows[:, t, :], chunk(CKV, t)[:, 0:KV_RANK],
                     rstd[:, N_MIX + t:N_MIX + t + 1]).then_inc(lat_rows, 1)
            act.wait_ge(lat_rows, 4)
            for t in range(TT):
                squares(ckv_rows[:, t, :], KV_RANK, N_CKV + t, prob[:, 2 + t, 0:KV_RANK])
            high_unit(7)
            act.wait_ge(gcol_landed, 32)
            for k in range(5):
                if k % 2 == 0:
                    act.wait_ge(latT, k // 2 + 1)
                copy(lat_hi[:, k, :], ps[:, 4 + k // 2, (k % 2) * SEQ:(k % 2 + 1) * SEQ],
                     gcol[:, KT + k:KT + k + 1]).then_inc(latT_hi, 1)
            high_unit(8)
            high_unit(9)
            high_unit(10)
            qkT_copy(0)
            qkT_copy(1)
            high_unit(11)
            high_unit(12)
            qkT_copy(2)
            qkT_copy(3)
            for t in range(TT):
                copy(v_a[:, t, :], chunk(VA, t), rstd[:, N_MIX + t:N_MIX + t + 1]).then_inc(act_read, 1)
            high_unit(13)
            up_both(QB0)
            high_unit(14)
            up_both(QB1)
            high_unit(15)
            qkT_copy(4)
            qkT_copy(5)
            up_both(KVB0)
            high_unit(16)
            qkT_copy(6)
            qkT_copy(7)

            def exps(g):
                path, t, heads = GROUPS[g]
                keys = P * (t + 1)
                act.wait_ge(max_ready, g + 1)
                if g >= 2:
                    act.wait_ge(p_turned, g - 1)
                for i, h in enumerate(heads):
                    e = nc.scalar.activation(prob[:, g % 2, i * keys:(i + 1) * keys],
                                             ps[:, 4 + g % 2, i * keys:(i + 1) * keys], ACT.Exp,
                                             bias=negmax[:, g, i:i + 1],
                                             accum_out=rowsum[:, 2 * path + t, h:h + 1])
                e.then_inc(p_ready, 1)

            def tanh_rows(q):
                for t in range(TT):
                    act.wait_ge(gate_lin, TT * q + t + 1)
                    nc.scalar.activation(gates[:, t, q * HALF:(q + 1) * HALF],
                                         gates[:, t, q * HALF:(q + 1) * HALF], ACT.Tanh,
                                         scale=0.5).then_inc(gate_done, 1)

            def oT_high(j):
                path, t = divmod(j, 2)
                act.wait_ge(o_turned, j + 1)
                copy(oT_hi[:, path, :, t * P:(t + 1) * P],
                     ps[:, 6, :].rearrange("p (b s) -> p b s", b=4)).then_inc(oT_hi_done, 1)

            for s in range(STEPS):
                if s == 0:
                    up_both(KVB1)
                if s < 2:
                    qkT_copy(8 + 2 * s)
                    qkT_copy(9 + 2 * s)
                if s in O_STEP:
                    oT_high(O_STEP.index(s))
                if 0 <= s - G_SLOT < NG:
                    exps(s - G_SLOT)
                high(U_GATE + AHEAD + s // 2, s % 2)
                if s % 4 == 3 and s > 3:
                    tanh_rows(s // 4 - 1)
            tanh_rows(NGATE - 1)

            def turned_high(j, done, ready, t, half, scale=1.0):
                act.wait_ge(done, j + 1)
                copy(xT_hi[:, 4 * half:4 * half + 4, t * P:(t + 1) * P],
                     ps[:, 4 + j, :].rearrange("p (b s) -> p b s", b=4), scale).then_inc(ready, 1)

            high_unit(25)
            turned_high(0, m_turned, mT_hi, 0, 0, 0.5)
            turned_high(1, m_turned, mT_hi, 0, 1, 0.5)
            high_unit(26)
            high_unit(27)
            turned_high(2, m_turned, mT_hi, 1, 0, 0.5)
            high_unit(28)
            high_unit(29)
            turned_high(3, m_turned, mT_hi, 1, 1, 0.5)

            def res_squares(i, done, col):
                act.wait_ge(done, i + 1)
                t, n = divmod(i, 2)
                squares(xs[:, t, n * HALF:(n + 1) * HALF], HALF, col + i, prob[:, i, :])

            res_squares(0, res_done, SSQ_MLP)
            res_squares(1, res_done, SSQ_MLP)
            high(30, 0)
            turned_high(0, h_turned, hT_hi, 0, 0)
            turned_high(1, h_turned, hT_hi, 0, 1)
            high(30, 1)
            high(31, 0)
            res_squares(2, res_done, SSQ_MLP)
            high(31, 1)
            res_squares(3, res_done, SSQ_MLP)
            high_unit(32)
            turned_high(2, h_turned, hT_hi, 1, 0)
            turned_high(3, h_turned, hT_hi, 1, 1)

            def high_ff(c, j, h):
                s = (U_FF + j) % SLOTS
                if h == 0:
                    act.wait_ge(raw_landed[s], c * 16 + 16 * ((U_FF + j) // SLOTS + 1))
                    if j == 3:
                        act.wait_ge(w2_used, c * 2)
                    elif j < 6:
                        act.wait_ge(u_done, c * 2 + j - 3)
                    else:
                        act.wait_ge(w2_used, c * 2 + 1)
                w = SLOT_W // 2
                copy(whi[:, s, h * w:(h + 1) * w], raw[:, s, h * w:(h + 1) * w]).then_inc(whi_ready, 1)

            def relu(c, p):
                act.wait_ge(u_done, c * 2 + p + 1)
                nc.scalar.activation(prob[:, p, :], ps[:, 4 + p, :], ACT.Relu).then_inc(u_relu, 1)

            def u_high(c, p):
                act.wait_ge(u_sq, c * 2 + p + 1)
                copy(lat_hi[:, 2 * p:2 * p + 2, :].rearrange("p a b -> p (a b)"), prob[:, 2 + p, :])\
                    .then_inc(uT_hi_done, 1)

            def mlp_chunk(c, last=False):
                high_ff(c, 3, 0)
                high_ff(c, 3, 1)
                for p in range(2):
                    relu(c, p)
                    if not last:
                        high_ff(c, 4 + p, 0)
                    u_high(c, p)
                    if not last:
                        high_ff(c, 4 + p, 1)
                if not last:
                    high_ff(c, 6, 0)
                    high_ff(c, 6, 1)

            for t in range(TT):
                relu(0, t)
                high(U_FF + 3 + t, 0)
                act.wait_ge(u_turned, t + 1)
                copy(lat_hi[:, 0:4, t * P:(t + 1) * P], ps[:, 6 + t, :].rearrange("p (b s) -> p b s", b=4))\
                    .then_inc(uT_hi_done, 1)
                high(U_FF + 3 + t, 1)
            high_unit(U_FF + 5)
            high_unit(U_FF + 6)
            with act.Fori(1, FF_CHUNKS - 1) as c:
                mlp_chunk(c)
            mlp_chunk(FF_CHUNKS - 1, last=True)

            def final_half(t):
                act.wait_ge(fin_scaled, 2 * t + 2)
                act.wait_ge(rstd_done, RSTD_FIN + t)
                copy(final_rows[:, t, HALF:D], final_rows[:, t, HALF:D],
                     rstd[:, N_FIN + t:N_FIN + t + 1]).then_inc(fin_rows_act, 1)

            for i in range(2 * TT):
                res_squares(i, fin_res, SSQ_FIN)
                if i == 2:
                    final_half(0)
            final_half(1)
            act.wait_ge(fin_rows_act, 2)
            act.dma_start(out_v[:, 1, HALF:D], final_rows[:, 1, HALF:D]).then_inc(out_stored_act, 16)

        @block.vector
        def _(dve):
            def low(u, h):
                s, w = u % SLOTS, unit_width(u) // 2
                dve.wait_ge(whi_ready, 2 * u + h + 1)
                nc.vector.tensor_tensor(wlo[:, s, h * w:(h + 1) * w], raw[:, s, h * w:(h + 1) * w],
                                        whi[:, s, h * w:(h + 1) * w].bitcast(F32),
                                        ALU.subtract).then_inc(wlo_ready, 1)

            def low_unit(u):
                low(u, 0)
                low(u, 1)

            def chunk(c, t):
                dve.wait_ge(chunk_done, TT * c + t + 1)
                return ps[:, 2 * (c % 2) + t, 0:SHAPE[c][0]]

            n_rot = [0]

            def rotate(src, dst, tab, t, r, heads, dim, tmp_a, tmp_b, done, before):
                if before:
                    dve.wait_ge(done, before)
                half = dim // 2
                shape = dict(h=heads)
                a = tmp_a.rearrange("p (h n) -> p h n", **shape)
                b = tmp_b.rearrange("p (h n) -> p h n", **shape)
                cos, sin = bcast(tab[:, 0, t, :], heads), bcast(tab[:, 1, t, :], heads)
                nc.vector.scalar_tensor_tensor(out=a, in0=src, scalar=r, in1=cos, op0=ALU.mult, op1=ALU.mult)
                nc.vector.scalar_tensor_tensor(out=b[:, :, 0:half], in0=src[:, :, half:dim], scalar=r,
                                               in1=sin[:, :, 0:half], op0=ALU.mult, op1=ALU.mult)
                nc.vector.scalar_tensor_tensor(out=b[:, :, half:dim], in0=src[:, :, 0:half], scalar=r,
                                               in1=sin[:, :, half:dim], op0=ALU.mult,
                                               op1=ALU.mult).then_inc(rope_part, 1)
                n_rot[0] += 1
                dve.wait_ge(rope_part, n_rot[0])
                nc.vector.tensor_tensor(dst, a, b, ALU.add).then_inc(done, 1)

            def rotate_a(c):
                for t in range(TT):
                    src = chunk(c, t).rearrange("p (h n) -> p h n", h=A_HEADS)
                    col = (N_MIX if c == KA else R_QA) + t
                    slot = 2 * (c - KA) + t
                    rotate(src, rows[:, slot, :].rearrange("p (h n) -> p h n", h=A_HEADS), tab_a, t,
                           rstd[:, col:col + 1], A_HEADS, A_DIM, prob[:, 0, :],
                           prob[:, 1, :], rows_dve, slot)

            def rotate_qb(c):
                for t in range(TT):
                    src = chunk(c, t).rearrange("p (h n) -> p h n", h=4)[:, :, B_NOPE:B_QK]
                    slot = 2 * (c - QB0) + t
                    dve.wait_ge(rows_act, slot + 1)
                    dst = rows[:, slot, 0:4 * B_QK].rearrange("p (h n) -> p h n", h=4)[:, :, B_NOPE:B_QK]
                    rotate(src, dst, tab_b, t, rstd[:, R_QB + t:R_QB + t + 1], 4, B_ROPE,
                           prob[:, 0, 0:4 * B_ROPE], prob[:, 1, 0:4 * B_ROPE], rows_dve, 4 + slot)

            def spread_kb(c):
                for t in range(TT):
                    slot = 2 * (c - KVB0) + t
                    dve.wait_ge(qk_turned, 4 + slot + 1)
                    dst = rows[:, slot, 0:4 * B_QK].rearrange("p (h n) -> p h n", h=4)[:, :, B_NOPE:B_QK]
                    nc.vector.tensor_copy(dst, bcast(k_rope[:, t, :], 4)).then_inc(rows_dve, 1)

            dve.wait_ge(gmix_landed, 16)
            for k in range(KT):
                dve.wait_ge(xT_hi_done, k // 2 * 2 + 2)
                nc.vector.scalar_tensor_tensor(out=xT_lo[:, k, :],
                                               in0=ps[:, 4 + k // 2, (k % 2) * SEQ:(k % 2 + 1) * SEQ],
                                               scalar=gcol[:, k:k + 1], in1=xT_hi[:, k, :].bitcast(F32),
                                               op0=ALU.mult, op1=ALU.subtract).then_inc(xT_lo_done, 1)
                if k in (1, 3):
                    low(0, k // 2)
            for u in range(1, 7):
                low_unit(u)
            dve.wait_ge(tab_landed, 32)
            dve.wait_ge(rstd_done, RSTD_MIX)
            for t in range(TT):
                dve.wait_ge(lat_rows, 3 + t)
                rotate(chunk(CKV, t)[:, KV_RANK:CKV_W].rearrange("p (h n) -> p h n", h=1),
                       k_rope[:, t:t + 1, :], tab_b, t, rstd[:, N_MIX + t:N_MIX + t + 1], 1, B_ROPE,
                       k_tmp[:, 0, :], k_tmp[:, 1, :], krope_done, t)
            low_unit(7)
            dve.wait_ge(gcol_landed, 32)
            for k in range(5):
                dve.wait_ge(latT_hi, min(k // 2 * 2 + 2, 5))
                nc.vector.scalar_tensor_tensor(out=lat_lo[:, k, :],
                                               in0=ps[:, 4 + k // 2, (k % 2) * SEQ:(k % 2 + 1) * SEQ],
                                               scalar=gcol[:, KT + k:KT + k + 1],
                                               in1=lat_hi[:, k, :].bitcast(F32),
                                               op0=ALU.mult, op1=ALU.subtract).then_inc(latT_lo, 1)
            low_unit(8)
            rotate_a(KA)
            low_unit(9)
            low_unit(10)
            dve.wait_ge(rstd_done, RSTD_QA)
            rotate_a(QA)
            low_unit(11)
            low_unit(12)
            low_unit(13)
            dve.wait_ge(rstd_done, RSTD_QB)
            rotate_qb(QB0)
            low_unit(14)
            rotate_qb(QB1)
            low_unit(15)
            dve.wait_ge(krope_done, 2)
            spread_kb(KVB0)
            low_unit(16)

            def row_max(g):
                path, t, heads = GROUPS[g]
                dve.wait_ge(scored, g + 1)
                nc.vector.tensor_reduce(negmax[:, g, 0:len(heads)],
                                        ps[:, 4 + g % 2, :].rearrange("p (h k) -> p h k", h=len(heads)),
                                        AX_X, ALU.max, negate=True).then_inc(max_ready, 1)

            def pT_copy(g):
                dve.wait_ge(p_turned, g + 1)
                if g >= 2:
                    dve.wait_ge(pv_done, g - 1)
                nc.vector.tensor_copy(prob[:, 2 + g % 2, :], ps[:, 6, :]).then_inc(pT_ready, 1)

            def o_norm(j):
                g_last = O_GROUP[j]
                dve.wait_ge(p_ready, g_last + 1)
                nc.vector.reciprocal(rrow[:, j, :], rowsum[:, j, :]).then_inc(rrow_ready, 1)
                dve.wait_ge(rrow_ready, j + 1)
                dve.wait_ge(pv_done, g_last + 1)
                nc.vector.tensor_tensor(rows[:, j, :].rearrange("p (h n) -> p h n", h=8),
                                        ps[:, 7, :].rearrange("p (h n) -> p h n", h=8),
                                        rrow[:, j, :].unsqueeze(2).broadcast_to([P, 8, 64]),
                                        ALU.mult).then_inc(o_rows, 1)

            def oT_low(j):
                path, t = divmod(j, 2)
                dve.wait_ge(oT_hi_done, j + 1)
                nc.vector.tensor_tensor(oT_lo[:, path, :, t * P:(t + 1) * P],
                                        ps[:, 6, :].rearrange("p (b s) -> p b s", b=4),
                                        oT_hi[:, path, :, t * P:(t + 1) * P].bitcast(F32),
                                        ALU.subtract).then_inc(oT_lo_done, 1)

            def gate_rows(q):
                for t in range(TT):
                    g = gates[:, t, q * HALF:(q + 1) * HALF]
                    nc.vector.scalar_tensor_tensor(out=g, in0=chunk(GATE0 + q, t),
                                                   scalar=rstd[:, N_MIX + t:N_MIX + t + 1], in1=g,
                                                   op0=ALU.mult, op1=ALU.add).then_inc(gate_lin, 1)

            for s in range(STEPS):
                if s == 0:
                    spread_kb(KVB1)
                if s in O_STEP:
                    oT_low(O_STEP.index(s))
                if 0 <= s - G_SLOT < NG:
                    row_max(s - G_SLOT)
                if s - G_SLOT - 2 in O_GROUP:
                    o_norm(O_GROUP.index(s - G_SLOT - 2))
                if 0 <= s - G_SLOT - 1 < NG:
                    pT_copy(s - G_SLOT - 1)
                low(U_GATE + AHEAD + s // 2, s % 2)
                if s % 4 == 1 and s > 1:
                    if s == 5:
                        dve.wait_ge(bias_landed, 32)
                    gate_rows(s // 4 - 1)
            gate_rows(NGATE - 1)

            def gated(i):
                t, n = divmod(i, 2)
                if i:
                    dve.wait_ge(m_rows, i)
                for path in range(2):
                    q = 2 * path + n
                    dve.wait_ge(gate_done, TT * q + t + 1)
                    dve.wait_ge(y_done, 2 * i + path + 1)
                    m = nc.vector.scalar_tensor_tensor(out=prob[:, path, :],
                                                       in0=gates[:, t, q * HALF:(q + 1) * HALF],
                                                       scalar=1.0, in1=ps[:, Y_BANK[i] + path, :],
                                                       op0=ALU.add, op1=ALU.mult)
                m.then_inc(m_part, 1)
                dve.wait_ge(m_part, i + 1)
                nc.vector.tensor_tensor(rows[:, i, :], prob[:, 0, :], prob[:, 1, :], ALU.add)\
                    .then_inc(m_rows, 1)

            def turned_low(j, hi_done, ready, t, half, scale):
                dve.wait_ge(hi_done, j + 1)
                nc.vector.scalar_tensor_tensor(out=xT_lo[:, 4 * half:4 * half + 4, t * P:(t + 1) * P],
                                               in0=ps[:, 4 + j, :].rearrange("p (b s) -> p b s", b=4),
                                               scalar=scale,
                                               in1=xT_hi[:, 4 * half:4 * half + 4, t * P:(t + 1) * P].bitcast(F32),
                                               op0=ALU.mult, op1=ALU.subtract).then_inc(ready, 1)

            low_unit(25)
            gated(0)
            gated(1)
            turned_low(0, mT_hi, mT_lo, 0, 0, 0.5)
            gated(2)
            turned_low(1, mT_hi, mT_lo, 0, 1, 0.5)
            low_unit(26)
            low_unit(27)
            gated(3)
            turned_low(2, mT_hi, mT_lo, 1, 0, 0.5)
            low_unit(28)
            low_unit(29)
            turned_low(3, mT_hi, mT_lo, 1, 1, 0.5)

            def residual(i, done, ready):
                t, n = divmod(i, 2)
                dve.wait_ge(done, i + 1)
                xr = xs[:, t, n * HALF:(n + 1) * HALF]
                nc.vector.tensor_tensor(xr, ps[:, ROW_BANK[i], :], xr, ALU.add).then_inc(ready, 1)

            def h_norm(t):
                if t == 0:
                    dve.wait_ge(grow_landed, 32)
                dve.wait_ge(rstd_done, RSTD_MLP + t)
                dve.wait_ge(m_turned, 2 * t + 2)
                nc.vector.scalar_tensor_tensor(out=rows[:, 2 * t:2 * t + 2, :].rearrange("p a b -> p (a b)"),
                                               in0=xs[:, t, :], scalar=rstd[:, N_MLP + t:N_MLP + t + 1],
                                               in1=g_mlp_row, op0=ALU.mult, op1=ALU.mult)\
                    .then_inc(h_rows, 1)

            residual(0, mix_done, res_done)
            residual(1, mix_done, res_done)
            dve.wait_ge(res_done, 2)
            h_norm(0)
            residual(2, mix_done, res_done)
            low(30, 0)
            turned_low(0, hT_hi, hT_lo, 0, 0, 1.0)
            turned_low(1, hT_hi, hT_lo, 0, 1, 1.0)
            low(30, 1)
            low(31, 0)
            residual(3, mix_done, res_done)
            low(31, 1)
            dve.wait_ge(res_done, 4)
            h_norm(1)
            low(32, 0)
            turned_low(2, hT_hi, hT_lo, 1, 0, 1.0)
            turned_low(3, hT_hi, hT_lo, 1, 1, 1.0)
            low(32, 1)

            def low_ff(c, j, h):
                s, w = (U_FF + j) % SLOTS, SLOT_W // 2
                dve.wait_ge(whi_ready, c * 8 + 2 * (U_FF + j) + h + 1)
                nc.vector.tensor_tensor(wlo[:, s, h * w:(h + 1) * w], raw[:, s, h * w:(h + 1) * w],
                                        whi[:, s, h * w:(h + 1) * w].bitcast(F32),
                                        ALU.subtract).then_inc(wlo_ready, 1)

            def square(c, p):
                dve.wait_ge(u_relu, c * 2 + p + 1)
                nc.vector.scalar_tensor_tensor(out=prob[:, 2 + p, :], in0=ps[:, 4 + p, :], scalar=0.0,
                                               in1=prob[:, p, :], op0=ALU.max, op1=ALU.mult)\
                    .then_inc(u_sq, 1)

            def u_low(c, p):
                dve.wait_ge(uT_hi_done, c * 2 + p + 1)
                nc.vector.tensor_tensor(lat_lo[:, 2 * p:2 * p + 2, :].rearrange("p a b -> p (a b)"),
                                        prob[:, 2 + p, :],
                                        lat_hi[:, 2 * p:2 * p + 2, :].rearrange("p a b -> p (a b)").bitcast(F32),
                                        ALU.subtract).then_inc(uT_lo_done, 1)

            def mlp_chunk(c, last=False):
                low_ff(c, 3, 0)
                low_ff(c, 3, 1)
                for p in range(2):
                    square(c, p)
                    if not last:
                        low_ff(c, 4 + p, 0)
                    u_low(c, p)
                    if not last:
                        low_ff(c, 4 + p, 1)
                if not last:
                    low_ff(c, 6, 0)
                    low_ff(c, 6, 1)

            for t in range(TT):
                square(0, t)
                low(U_FF + 3 + t, 0)
                dve.wait_ge(uT_hi_done, t + 1)
                nc.vector.tensor_tensor(lat_lo[:, 0:4, t * P:(t + 1) * P],
                                        ps[:, 6 + t, :].rearrange("p (b s) -> p b s", b=4),
                                        lat_hi[:, 0:4, t * P:(t + 1) * P].bitcast(F32),
                                        ALU.subtract).then_inc(uT_lo_done, 1)
                low(U_FF + 3 + t, 1)
            low_unit(U_FF + 5)
            low_unit(U_FF + 6)
            with dve.Fori(1, FF_CHUNKS - 1) as c:
                mlp_chunk(c)
            mlp_chunk(FF_CHUNKS - 1, last=True)

            def final_scaled(i):
                t, n = divmod(i, 2)
                dve.wait_ge(fin_res, i + 1)
                cols = slice(n * HALF, (n + 1) * HALF)
                nc.vector.tensor_tensor(final_rows[:, t, cols], xs[:, t, cols], g_fin_row[:, cols],
                                        ALU.mult).then_inc(fin_scaled, 1)

            def final_half(t):
                dve.wait_ge(fin_scaled, 2 * t + 1)
                dve.wait_ge(rstd_done, RSTD_FIN + t)
                nc.vector.tensor_scalar(final_rows[:, t, 0:HALF], final_rows[:, t, 0:HALF],
                                        rstd[:, N_FIN + t:N_FIN + t + 1], None, ALU.mult)\
                    .then_inc(fin_rows, 1)

            for i in range(2 * TT):
                residual(i, ff_done, fin_res)
                if i < 2:
                    final_scaled(i)
            final_half(0)
            final_scaled(2)
            final_scaled(3)
            final_half(1)

        @block.tensor
        def _(pe):
            def product(dst, a_hi, a_lo, b_hi, b_lo, start, stop):
                nc.tensor.matmul(dst, a_hi, b_hi, start=start, stop=False)
                nc.tensor.matmul(dst, a_hi, b_lo, start=False, stop=False)
                return nc.tensor.matmul(dst, a_lo, b_hi, start=False, stop=stop)

            def turn(bank, srcs, width, done):
                for b, src in enumerate(srcs):
                    m = nc.tensor.transpose(ps[0:width, bank, b * P:(b + 1) * P], src, ident[:, :])
                m.then_inc(done, 1)

            def blocks(ap, w=P):
                return [ap[:, b * w:(b + 1) * w] for b in range(4)]

            def proj(c, k):
                first, n, kts = UNITS_OF[c]
                w, kn = SHAPE[c]
                u = first + k // kts
                if k % kts == 0:
                    pe.wait_ge(wlo_ready, 2 * u + (1 if kts % 2 == 0 else 2))
                elif kts % 2 == 0 and k % kts == kts // 2:
                    pe.wait_ge(wlo_ready, 2 * u + 2)
                if k == 0 and c - 2 in ACT_READ:
                    pe.wait_ge(*ACT_READ[c - 2])
                if k == 0 and c - 2 in DVE_READ:
                    pe.wait_ge(*DVE_READ[c - 2])
                up = QB0 <= c <= KVB1
                a_hi, a_lo, k0 = (lat_hi, lat_lo, 0 if c < KVB0 else 3) if up else (xT_hi, xT_lo, 0)
                for t in range(TT):
                    m = product(ps[:, 2 * (c % 2) + t, 0:w],
                                a_hi[:, k0 + k, t * P:(t + 1) * P], a_lo[:, k0 + k, t * P:(t + 1) * P],
                                whi[:, u % SLOTS, k % kts * w:(k % kts + 1) * w],
                                wlo[:, u % SLOTS, k % kts * w:(k % kts + 1) * w],
                                k == 0, k == kn - 1)
                    if k == kn - 1:
                        m.then_inc(chunk_done, 1)
                if k % kts == kts - 1 and k < kn - 1:
                    m.then_inc(chunk_half, 1)

            def proj_all(c, start=0, end=None):
                for k in range(start, SHAPE[c][1] if end is None else end):
                    proj(c, k)

            def turn_qk(e):
                slot = e % 4
                pe.wait_ge(rows_dve, e + 1)
                if e >= 4:
                    pe.wait_ge(rows_act, e - 4 + 1)
                    pe.wait_ge(qkT_ready, e - 3)
                    turn(QK_BANK[e % 4], blocks(rows[:, slot, 0:4 * B_QK], B_QK), B_QK, qk_turned)
                else:
                    turn(QK_BANK[e % 4], blocks(rows[:, slot, :]), P, qk_turned)

            def turn_latents():
                pe.wait_ge(lat_rows, 4)
                tiles = [cq_rows[:, :, k * P:(k + 1) * P] for k in range(3)] + \
                        [ckv_rows[:, :, k * P:(k + 1) * P] for k in range(2)]
                turn(4, [tiles[k][:, t, :] for k in (0, 1) for t in range(TT)], P, latT)
                turn(5, [tiles[k][:, t, :] for k in (2, 3) for t in range(TT)], P, latT)
                turn(6, [tiles[k][:, t, :] for k in (4,) for t in range(TT)], P, latT)

            pe.wait_ge(const_ready, 3)
            for _ in range(WARM_UP):
                nc.tensor.matmul(ps[:, 0, 0:P], ident_h[:, :], causal[:, :], start=True, stop=True)
            for t in range(TT):
                pe.wait_ge(x_landed[t], 16)
            for b in range(4):
                turn(4 + b, [xs[:, t, k * P:(k + 1) * P] for k in (2 * b, 2 * b + 1) for t in range(TT)],
                     P, x_turned)
            for k in range(KT):
                pe.wait_ge(xT_lo_done, k + 1)
                proj(CQ, k)
            proj_all(CKV)
            proj_all(KA, 0, 6)
            turn_latents()
            proj_all(KA, 6)
            proj_all(QA, 0, 6)
            pe.wait_ge(latT_lo, 2)
            turn_qk(0)
            turn_qk(1)
            proj_all(QA, 6)
            proj_all(VA, 0, 6)
            pe.wait_ge(latT_lo, 5)
            turn_qk(2)
            turn_qk(3)
            proj_all(VA, 6)
            proj_all(QB0)
            proj_all(QB1)
            turn_qk(4)
            turn_qk(5)
            proj_all(KVB0)
            turn_qk(6)
            turn_qk(7)
            proj_all(KVB1)

            def scores(g):
                path, t, heads = GROUPS[g]
                keys, bank = P * (t + 1), 4 + g % 2
                if g < 2:
                    pe.wait_ge(qkT_ready, (10, 11)[g])
                else:
                    pe.wait_ge(p_ready, g - 1)
                if g == NG // 2:
                    pe.wait_ge(qkT_ready, 12)
                for i, h in enumerate(heads):
                    dst = ps[:, bank, i * keys:(i + 1) * keys]
                    if path == 0:
                        b = h % 2 * A_DIM
                        q, k = (qkT_a[b:b + A_DIM, w, h // 2, :] for w in range(2))
                    else:
                        q, k = (qkT_b[0:B_QK, w, h, :] for w in range(2))
                    nc.tensor.matmul(dst, q[:, t * P:(t + 1) * P], k[:, 0:keys], start=True, stop=False)
                    m = nc.tensor.matmul(dst[:, t * P:keys], ident_h[:, :], causal[:, :], start=False, stop=True)
                m.then_inc(scored, 1)

            def turn_p(g):
                pe.wait_ge(p_ready, g + 1)
                if g == 0:
                    pe.wait_ge(qkT_ready, 12)
                else:
                    pe.wait_ge(pT_ready, g)
                if g - 2 in O_GROUP:
                    pe.wait_ge(oT_lo_done, O_GROUP.index(g - 2) + 1)
                turn(6, blocks(prob[:, g % 2, :]), P, p_turned)

            def values(g):
                path, t, heads = GROUPS[g]
                pe.wait_ge(pT_ready, g + 1)
                if g == 0:
                    pe.wait_ge(act_read, 2)
                if g == NG // 2:
                    pe.wait_ge(rows_act, 8)
                if g - 1 in O_GROUP:
                    pe.wait_ge(o_rows, O_GROUP.index(g - 1) + 1)
                v = (v_a, v_b)[path]
                for i, h in enumerate(heads):
                    for kb in range(t + 1):
                        b = i * (t + 1) + kb
                        m = nc.tensor.matmul(ps[:, 7, h * 64:(h + 1) * 64], prob[:, 2 + g % 2, b * P:(b + 1) * P],
                                             v[:, kb, h * 64:(h + 1) * 64], start=(kb == 0), stop=(kb == t))
                m.then_inc(pv_done, 1)

            def turn_o(j):
                pe.wait_ge(o_rows, j + 1)
                pe.wait_ge(pT_ready, min(O_GROUP[j] + 2, NG))
                turn(6, blocks(rows[:, j, :]), P, o_turned)

            for s in range(STEPS):
                c, k = GATE0 + s // 4, 2 * (s % 4)
                if s == 1:
                    turn_qk(10)
                    turn_qk(11)
                if 0 < s - G_SLOT < NG:
                    scores(s - G_SLOT)
                proj(c, k)
                if s == 0:
                    turn_qk(8)
                    turn_qk(9)
                if 0 <= s - G_SLOT - 1 < NG:
                    turn_p(s - G_SLOT - 1)
                if s == G_SLOT:
                    scores(0)
                proj(c, k + 1)
                if 0 <= s - G_SLOT - 1 < NG:
                    values(s - G_SLOT - 1)
                if s + 1 in O_STEP:
                    turn_o(O_STEP.index(s + 1))

            def mixer_out(i):
                t, n = divmod(i, 2)
                for path in range(2):
                    u = U_WO + 2 * n + path
                    if t == 0:
                        pe.wait_ge(wlo_ready, 2 * u + 2)
                    if path == 0:
                        if i == 0:
                            pe.wait_ge(oT_lo_done, 4)
                            pe.wait_ge(gate_lin, TT * (NGATE - 1))
                        elif i == 1:
                            pe.wait_ge(gate_lin, TT * NGATE)
                        else:
                            pe.wait_ge(m_part, i - 1)
                    for k in range(4):
                        m = product(ps[:, Y_BANK[i] + path, :], oT_hi[:, path, k, t * P:(t + 1) * P],
                                    oT_lo[:, path, k, t * P:(t + 1) * P],
                                    whi[:, u % SLOTS, k * HALF:(k + 1) * HALF],
                                    wlo[:, u % SLOTS, k * HALF:(k + 1) * HALF], k == 0, k == 3)
                    m.then_inc(y_done, 1)

            def turn_m(i):
                pe.wait_ge(m_rows, i + 1)
                if i == 0:
                    pe.wait_ge(p_ready, NG)
                turn(4 + i, blocks(rows[:, i, :]), P, m_turned)

            def out_proj(i, k0, k1):
                t, n = divmod(i, 2)
                for k in range(k0, k1):
                    u = U_OUT + 2 * n + k // 4
                    if t == 0 and k % 4 == 0:
                        pe.wait_ge(wlo_ready, 2 * u + 2)
                    m = product(ps[:, ROW_BANK[i], :], xT_hi[:, k, t * P:(t + 1) * P], xT_lo[:, k, t * P:(t + 1) * P],
                                whi[:, u % SLOTS, k % 4 * HALF:(k % 4 + 1) * HALF],
                                wlo[:, u % SLOTS, k % 4 * HALF:(k % 4 + 1) * HALF], k == 0, k == KT - 1)
                if k1 == KT:
                    m.then_inc(mix_done, 1)

            mixer_out(0)
            mixer_out(1)
            turn_m(0)
            mixer_out(2)
            turn_m(1)
            mixer_out(3)
            turn_m(2)
            pe.wait_ge(mT_lo, 2)
            pe.wait_ge(m_part, 3)
            out_proj(0, 0, 4)
            turn_m(3)
            out_proj(0, 4, KT)
            out_proj(1, 0, KT)
            pe.wait_ge(mT_lo, 4)
            pe.wait_ge(m_part, 4)
            out_proj(2, 0, KT)

            def turn_h(t):
                pe.wait_ge(h_rows, t + 1)
                for half in range(2):
                    turn(4 + 2 * t + half, blocks(rows[:, 2 * t + half, :]), P, h_turned)

            turn_h(0)
            out_proj(3, 0, KT)

            def mlp_in(p):
                s = (U_FF + p) % SLOTS
                for f in range(2):
                    for k in range(KT):
                        w = slice(k * 256 + f * P, k * 256 + (f + 1) * P)
                        m = product(ps[:, 4 + p, f * SEQ:(f + 1) * SEQ], whi[:, s, w], wlo[:, s, w],
                                    xT_hi[:, k, :], xT_lo[:, k, :], k == 0, k == KT - 1)
                return m

            def mlp_out_tile(t, p, order, first, end):
                s = (U_FF + 2 + p) % SLOTS
                for f, n in order:
                    w = slice(f * D + n * HALF, f * D + (n + 1) * HALF)
                    a = (slice(None), 2 * p + f, slice(t * P, (t + 1) * P))
                    m = product(ps[:, ROW_BANK[2 * t + n], :], lat_hi[a], lat_lo[a], whi[:, s, w], wlo[:, s, w],
                                first and p == 0 and f == 0, end and f == 1)
                    if end and f == 1:
                        m.then_inc(ff_done, 1)
                return m

            def mlp_out(c, p, last):
                pe.wait_ge(wlo_ready, c * 8 + 2 * (U_FF + 2 + p) + 2)
                pe.wait_ge(uT_lo_done, c * 2 + p + 1)
                end = last and p == 1
                for t in range(TT):
                    m = mlp_out_tile(t, p, [(f, n) for n in range(2) for f in range(2)] if end else
                                     [(f, n) for f in range(2) for n in range(2)], False, end)
                if not end:
                    m.then_inc(w2_used, 1)

            def mlp_in_rows(t, p, k0=0, k1=KT):
                s = (U_FF + p) % SLOTS
                for k in range(k0, k1):
                    w = slice(k * 256, (k + 1) * 256)
                    m = product(ps[:, 4 + t, p * 256:(p + 1) * 256], xT_hi[:, k, t * P:(t + 1) * P],
                                xT_lo[:, k, t * P:(t + 1) * P], whi[:, s, w], wlo[:, s, w], k == 0, k == KT - 1)
                if p == 1 and k1 == KT:
                    m.then_inc(u_done, 1)

            def turn_u(t):
                pe.wait_ge(u_sq, t + 1)
                turn(6 + t, blocks(prob[:, 2 + t, :]), P, u_turned)

            pe.wait_ge(hT_lo, 2)
            pe.wait_ge(wlo_ready, 2 * U_FF + 2)
            mlp_in_rows(0, 0)
            pe.wait_ge(wlo_ready, 2 * U_FF + 3)
            mlp_in_rows(0, 1, 0, 4)
            pe.wait_ge(wlo_ready, 2 * U_FF + 4)
            mlp_in_rows(0, 1, 4, 6)
            turn_h(1)
            mlp_in_rows(0, 1, 6)
            pe.wait_ge(hT_lo, 3)
            mlp_in_rows(1, 0, 0, 4)
            pe.wait_ge(hT_lo, 4)
            mlp_in_rows(1, 0, 4)
            turn_u(0)
            mlp_in_rows(1, 1)
            pe.wait_ge(res_done, 4)
            for t in range(TT):
                pe.wait_ge(uT_lo_done, t + 1)
                for p in range(2):
                    if t == 0:
                        pe.wait_ge(wlo_ready, 2 * (U_FF + 2 + p) + 2)
                    m = mlp_out_tile(t, p, [(f, n) for f in range(2) for n in range(2)], True, False)
                    if t == 1:
                        m.then_inc(w2_used, 1)
                    elif p == 0:
                        turn_u(1)

            def mlp_chunk(c, last):
                for p in range(2):
                    pe.wait_ge(wlo_ready, c * 8 + 2 * (U_FF + p) + 2)
                    mlp_in(p).then_inc(u_done, 1)
                for p in range(2):
                    mlp_out(c, p, last)

            with pe.Fori(1, FF_CHUNKS - 1) as c:
                mlp_chunk(c, False)
            mlp_chunk(FF_CHUNKS - 1, True)


_INS = ["x", "g_mix", "w_in", "b_gate", "g_cq", "w_q_up", "g_ckv", "w_kv_up", "w_o_a", "w_o_b", "w_out",
        "g_mlp", "w_ff1", "w_ff2", "g_final"]
_OUTS = [((1, SEQ, D), "float32")]


def kernel(**inputs):
    import concourse.bacc as _bacc
    from concourse.bass_utils import run_bass_kernel_spmd as _run

    nc = _bacc.Bacc("TRN2", target_bir_lowering=False, num_devices=1)
    arrays, args = {}, []
    given = [(name, inputs[name]) for name in _INS]
    given += [("rope_a", rope_tables(A_DIM)), ("rope_b", rope_tables(B_ROPE))]
    for name, value in given:
        a = np.ascontiguousarray(value)
        arrays[f"in_{name}_dram"] = a
        args.append(nc.dram_tensor(f"in_{name}_dram", a.shape, mybir.dt.from_np(a.dtype), kind="ExternalInput").ap())
    for i, (shape, dtype) in enumerate(_OUTS):
        dt = mybir.dt.from_np(np.dtype(dtype))
        args.append(nc.dram_tensor(f"out_{i}_dram", shape, dt, kind="ExternalOutput").ap())
    hybrid_block(nc, *args)
    r = _run(nc, [arrays], core_ids=[0])
    return r.results[0]["out_0_dram"]
```
